# Optimizing a Trainium2 kernel written in Bass

```python
import math
import jax, jax.numpy as jnp
from jax import lax
import numpy as np

D_MODEL = 1024
BATCH = 1
SEQ = 512
DEPTH = 1

CHUNK = 64
Q_BLOCK = 128
N_HEADS = 8
QK_NOPE_DIM = 64
QK_ROPE_DIM = 32
V_HEAD_DIM = 64
Q_LORA_RANK = 512
KV_LORA_RANK = 256
MLA_WIDTH = N_HEADS * V_HEAD_DIM
ROPE_THETA = 10000.0
POOL_WINDOWS = (2, 4, 8, 16)
N_POOL_GROUPS = len(POOL_WINDOWS)
POOL_WIDTH = D_MODEL // 2
POOL_GROUP_DIM = POOL_WIDTH // N_POOL_GROUPS
MIX_WIDTH = MLA_WIDTH + POOL_WIDTH
IN_COLS = Q_LORA_RANK + KV_LORA_RANK + QK_ROPE_DIM + POOL_WIDTH
D_FF = 2816
LN_EPS = 1e-5
RMS_EPS = 1e-6
N_SUBLAYERS = 3
ALPHA = (2.0 * DEPTH) ** 0.25
BETA = (8.0 * DEPTH) ** -0.25

kernel_name = "hybrid_mla_multiscale_pool_macaron_deepnorm_adaln"

def _layernorm(x, g, b):
    xf = x.astype(jnp.float32)
    mu = jnp.mean(xf, axis=-1, keepdims=True)
    var = jnp.mean(jnp.square(xf - mu), axis=-1, keepdims=True)
    return ((xf - mu) * lax.rsqrt(var + LN_EPS) * g.astype(jnp.float32) + b.astype(jnp.float32)).astype(x.dtype)

def _rmsnorm(x, g):
    xf = x.astype(jnp.float32)
    ms = jnp.mean(jnp.square(xf), axis=-1, keepdims=True)
    return (xf * lax.rsqrt(ms + RMS_EPS) * g.astype(jnp.float32)).astype(x.dtype)

def _rope(x, cos, sin):
    x1, x2 = jnp.split(x, 2, axis=-1)
    return jnp.concatenate([x1 * cos - x2 * sin, x1 * sin + x2 * cos], axis=-1)

def _swiglu(h, w_in, w_out):
    g, u = jnp.split(h @ w_in, 2, axis=-1)
    return (jax.nn.silu(g) * u) @ w_out

def _mla(cq, ckv, k_rope_raw, positions, q_norm_g, kv_norm_g, w_uq, w_ukv):
    B, S, _ = cq.shape
    q = (_rmsnorm(cq, q_norm_g) @ w_uq).reshape(B, S, N_HEADS, QK_NOPE_DIM + QK_ROPE_DIM)
    kv = (_rmsnorm(ckv, kv_norm_g) @ w_ukv).reshape(B, S, N_HEADS, QK_NOPE_DIM + V_HEAD_DIM)
    q_nope, q_rope = q[..., :QK_NOPE_DIM], q[..., QK_NOPE_DIM:]
    k_nope, v = kv[..., :QK_NOPE_DIM], kv[..., QK_NOPE_DIM:]
    inv_freq = ROPE_THETA ** (-jnp.arange(0, QK_ROPE_DIM, 2, dtype=jnp.float32) / QK_ROPE_DIM)
    ang = positions.astype(jnp.float32)[..., None] * inv_freq
    cos = jnp.cos(ang).astype(cq.dtype)
    sin = jnp.sin(ang).astype(cq.dtype)
    q_rope = _rope(q_rope, cos[:, :, None, :], sin[:, :, None, :])
    k_rope = _rope(k_rope_raw, cos, sin)
    sm_scale = (QK_NOPE_DIM + QK_ROPE_DIM) ** -0.5
    key_chunk = jnp.arange(S) // CHUNK
    n_blocks = S // Q_BLOCK

    def attend_block(i):
        start = i * Q_BLOCK
        qn = lax.dynamic_slice_in_dim(q_nope, start, Q_BLOCK, axis=1)
        qr = lax.dynamic_slice_in_dim(q_rope, start, Q_BLOCK, axis=1)
        s = (jnp.einsum('bqhd,bkhd->bhqk', qn, k_nope)
             + jnp.einsum('bqhr,bkr->bhqk', qr, k_rope)).astype(jnp.float32) * sm_scale
        q_chunk = (start + jnp.arange(Q_BLOCK)) // CHUNK
        mask = key_chunk[None, :] <= q_chunk[:, None]
        s = jnp.where(mask[None, None], s, -jnp.inf)
        p = jax.nn.softmax(s, axis=-1).astype(v.dtype)
        return jnp.einsum('bhqk,bkhd->bqhd', p, v)

    out = lax.map(attend_block, jnp.arange(n_blocks))
    return jnp.moveaxis(out, 0, 1).reshape(B, S, MLA_WIDTH)

def _multiscale_pool(u, pool_w, pool_b, pool_scale):
    B, S, _ = u.shape
    ug = u.reshape(B, S, N_POOL_GROUPS, POOL_GROUP_DIM)
    cs = jnp.cumsum(ug.astype(jnp.float32), axis=1)
    t = jnp.arange(1, S + 1, dtype=jnp.float32)
    means = []
    for gi, w in enumerate(POOL_WINDOWS):
        prev = jnp.pad(cs[:, :-w, gi], ((0, 0), (w, 0), (0, 0)))
        cnt = jnp.minimum(t, float(w))[None, :, None]
        means.append((cs[:, :, gi] - prev) / cnt)
    pooled = jnp.stack(means, axis=2).astype(u.dtype) - ug
    y = jnp.einsum('bsgc,gcd->bsgd', pooled, pool_w) + pool_b
    return y.reshape(B, S, POOL_WIDTH) * pool_scale

def setup_inputs(seed: int = 0) -> dict:
    key = jax.random.key(seed)
    ks = jax.random.split(key, 24)
    f32 = jnp.float32

    def nrm(k, shape, scale):
        return jax.random.normal(k, shape, f32) * scale

    x = jax.random.normal(ks[0], (BATCH, SEQ, D_MODEL), f32)
    c = jax.random.normal(ks[1], (BATCH, D_MODEL), f32)
    offsets = jax.random.randint(ks[2], (BATCH, 1), 0, 1024, dtype=jnp.int32)
    positions = offsets + jnp.arange(SEQ, dtype=jnp.int32)[None, :]
    return {
        'x': x,
        'c': c,
        'positions': positions,
        'ln_in_g': 1.0 + nrm(ks[3], (D_MODEL,), 0.02),
        'ln_in_b': nrm(ks[4], (D_MODEL,), 0.02),
        'w_ada': nrm(ks[5], (DEPTH, D_MODEL, N_SUBLAYERS * 3 * D_MODEL), 0.5 * D_MODEL ** -0.5),
        'b_ada': nrm(ks[6], (DEPTH, N_SUBLAYERS * 3 * D_MODEL), 0.02),
        'ffn1_w_in': nrm(ks[7], (DEPTH, D_MODEL, 2 * D_FF), D_MODEL ** -0.5),
        'ffn1_w_out': nrm(ks[8], (DEPTH, D_FF, D_MODEL), BETA * D_FF ** -0.5),
        'w_in': nrm(ks[9], (DEPTH, D_MODEL, IN_COLS), D_MODEL ** -0.5),
        'q_norm_g': 1.0 + nrm(ks[10], (DEPTH, Q_LORA_RANK), 0.02),
        'kv_norm_g': 1.0 + nrm(ks[11], (DEPTH, KV_LORA_RANK), 0.02),
        'w_uq': nrm(ks[12], (DEPTH, Q_LORA_RANK, N_HEADS * (QK_NOPE_DIM + QK_ROPE_DIM)), Q_LORA_RANK ** -0.5),
        'w_ukv': nrm(ks[13], (DEPTH, KV_LORA_RANK, N_HEADS * (QK_NOPE_DIM + V_HEAD_DIM)), KV_LORA_RANK ** -0.5),
        'pool_w': nrm(ks[14], (DEPTH, N_POOL_GROUPS, POOL_GROUP_DIM, POOL_GROUP_DIM), POOL_GROUP_DIM ** -0.5),
        'pool_b': nrm(ks[15], (DEPTH, N_POOL_GROUPS, POOL_GROUP_DIM), 0.02),
        'pool_scale': 1.0 + nrm(ks[16], (DEPTH, POOL_WIDTH), 0.02),
        'w_out': nrm(ks[17], (DEPTH, MIX_WIDTH, D_MODEL), BETA * MIX_WIDTH ** -0.5),
        'ffn2_w_in': nrm(ks[18], (DEPTH, D_MODEL, 2 * D_FF), D_MODEL ** -0.5),
        'ffn2_w_out': nrm(ks[19], (DEPTH, D_FF, D_MODEL), BETA * D_FF ** -0.5),
        'post_ln_g': 1.0 + nrm(ks[20], (DEPTH, N_SUBLAYERS, D_MODEL), 0.02),
        'post_ln_b': nrm(ks[21], (DEPTH, N_SUBLAYERS, D_MODEL), 0.02),
    }

def reference(x, c, positions, ln_in_g, ln_in_b, w_ada, b_ada, ffn1_w_in, ffn1_w_out,
              w_in, q_norm_g, kv_norm_g, w_uq, w_ukv, pool_w, pool_b, pool_scale, w_out,
              ffn2_w_in, ffn2_w_out, post_ln_g, post_ln_b):
    B, S, D = x.shape
    x = _layernorm(x, ln_in_g, ln_in_b)
    c_act = jax.nn.silu(c)
    split_at = [Q_LORA_RANK, Q_LORA_RANK + KV_LORA_RANK, Q_LORA_RANK + KV_LORA_RANK + QK_ROPE_DIM]
    for l in range(DEPTH):
        mod = (c_act @ w_ada[l] + b_ada[l]).reshape(B, N_SUBLAYERS, 3, D)
        shift, scale, gate = mod[:, :, 0], mod[:, :, 1], mod[:, :, 2]

        h = x * (1.0 + scale[:, 0, None, :]) + shift[:, 0, None, :]
        y = _swiglu(h, ffn1_w_in[l], ffn1_w_out[l])
        x = _layernorm(ALPHA * x + 0.5 * gate[:, 0, None, :] * y, post_ln_g[l, 0], post_ln_b[l, 0])

        h = x * (1.0 + scale[:, 1, None, :]) + shift[:, 1, None, :]
        proj = h @ w_in[l]
        cq, ckv, k_rope_raw, u = jnp.split(proj, split_at, axis=-1)
        attn = _mla(cq, ckv, k_rope_raw, positions, q_norm_g[l], kv_norm_g[l], w_uq[l], w_ukv[l])
        pooled = _multiscale_pool(u, pool_w[l], pool_b[l], pool_scale[l])
        y = jnp.concatenate([attn, pooled], axis=-1) @ w_out[l]
        x = _layernorm(ALPHA * x + gate[:, 1, None, :] * y, post_ln_g[l, 1], post_ln_b[l, 1])

        h = x * (1.0 + scale[:, 2, None, :]) + shift[:, 2, None, :]
        y = _swiglu(h, ffn2_w_in[l], ffn2_w_out[l])
        x = _layernorm(ALPHA * x + 0.5 * gate[:, 2, None, :] * y, post_ln_g[l, 2], post_ln_b[l, 2])
    return x


_drawn_inputs = setup_inputs


def setup_inputs(seed=0):
    import zlib

    import numpy as np

    out = dict(_drawn_inputs(seed))
    spreads = {}
    factors = {'ln_in_g': 3.003,
     'ln_in_b': 2.864,
     'b_ada': 5.94,
     'q_norm_g': 8.0,
     'kv_norm_g': 8.0,
     'w_uq': 5.049,
     'pool_b': 8.0,
     'pool_scale': 8.0}
    for name, (base, spread) in spreads.items():
        noise = np.random.default_rng([zlib.crc32(name.encode()), seed]).standard_normal(out[name].shape)
        drawn = base * np.exp(spread * noise) if base else spread * noise
        out[name] = __import__('jax').numpy.asarray(drawn.astype(out[name].dtype))
    for name, factor in factors.items():
        out[name] = (out[name] * factor).astype(out[name].dtype)
    return out
```

```python
import math
from contextlib import ExitStack

import numpy as np

import concourse.bass as bass
from concourse import mybir

P = 128
TOK = 512
D = 1024
KD = D // P
D_FF = 2816
FT = D_FF // P
HEADS, NOPE, ROPE, VDIM = 8, 64, 32, 64
QR, KVR = 512, 256
KQ, KKV = QR // P, KVR // P
WINDOWS = (2, 4, 8, 16)
NPG = len(WINDOWS)
PADW = 16
CHUNK = 64
QB = TOK // P
ALPHA = 2.0 ** 0.25
LN_EPS, RMS_EPS = 1e-5, 1e-6
SM_SCALE = (NOPE + ROPE) ** -0.5
MASKED = -3.0e38

SLOTS = 4
UNIT = KD * P
UP = 2 * FT
DPM = 3
DOWN = DPM * KD
N_PROJ = 2 + 1 + KQ + NPG
MIX = N_PROJ + 1 + 1 + HEADS // 2 + KD
F1 = 0
F1_DOWN = F1 + UP
MX = F1_DOWN + DOWN
U_KNOPE = MX + N_PROJ
U_V = U_KNOPE + 1
U_UQ = U_V + 1
U_OUT = U_UQ + HEADS // 2
F2 = MX + MIX
F2_DOWN = F2 + UP
UNITS = F2_DOWN + DOWN
LAST_K = FT - 8 * (DPM - 1)


def _slots():
    out, base = [], 0
    for n in range(UNITS):
        if n == F1_DOWN or n == F2_DOWN:
            base = out[n - SLOTS]
        if F1_DOWN <= n < MX:
            out.append((base + (n - F1_DOWN) % DPM) % SLOTS)
        elif n >= F2_DOWN:
            out.append((base + (n - F2_DOWN) % DPM) % SLOTS)
        elif n == MX:
            out.append((base + DPM) % SLOTS)
        elif n == 0:
            out.append(0)
        else:
            out.append((out[-1] + 1) % SLOTS)
    return out


SLOT = _slots()
PREV = [max((m for m in range(n) if SLOT[m] == SLOT[n]), default=None) for n in range(UNITS)]
FILL = [sum(SLOT[m] == SLOT[n] for m in range(n + 1)) for n in range(UNITS)]

C_LNG = 0
C_LNB = C_LNG + 4 * KD
C_BADA = C_LNB + 4 * KD
C_QG = C_BADA + 9 * KD
C_KVG = C_QG + KQ
C_PB = C_KVG + KKV
C_PS = C_PB + NPG
C_FREQ = C_PS + NPG
C_SIGN = C_FREQ + 1
C_RCNT = C_SIGN + 1
C_ID = C_RCNT + PADW
COLS = C_ID + P
ADA = 9 * KD
ADA_FIRST = 2 * KD


POOLED = [sum(d + 1 + 3 for d in range(g + 1)) for g in range(NPG)]
MAGIC = 1.5 * 2.0 ** 23


def _parts(value, bits):
    out = []
    for b in bits:
        if b:
            q = 2.0 ** (b - 1 - math.floor(math.log2(abs(value))))
            p = round(value * q) / q
        else:
            p = float(np.float32(value))
        out.append(p)
        value -= p
    return out


def _mod_two_pi(exponent):
    one = 10 ** 40
    two_pi = 2 * 31415926535897932384626433832795028841971
    r = 2 ** exponent * one % two_pi
    return (r - two_pi if 2 * r > two_pi else r) / one


TWO_PI_PARTS = _parts(2.0 * math.pi, (12, 12, 0))
PI12_PARTS = _parts(_mod_two_pi(12), (12, 0))
PI22_PARTS = _parts(_mod_two_pi(22), (12, 0))
PI_CLAMP = 3.1415925
ROPE_STEPS = 2 + 2 + 1 + 2 + 1 + 4 * (2 + len(TWO_PI_PARTS)) + 4 + 2 + 1


def unit_width(n):
    for down, end in ((F1_DOWN, MX), (F2_DOWN, UNITS)):
        if down <= n < end and (n - down) % DPM == DPM - 1:
            return LAST_K * P
    return UNIT


def affine(f, i, lo, hi):
    if isinstance(i, int):
        return f(i)
    base, step = f(lo), (f(lo + 1) - f(lo) if hi - lo > 1 else 0)
    assert all(f(k) == base + step * (k - lo) for k in range(lo, hi)), "not affine"
    return i * step + (base - step * lo)


def build(nc, xT, wunits, ada_w, c_rows, pos_rows, cols_dram, pool_w, outT):
    F32, F32R, BF16, I32 = (mybir.dt.float32, mybir.dt.float32r, mybir.dt.bfloat16, mybir.dt.int32)
    ALU, ACT, AX = mybir.AluOpType, mybir.ActivationFunctionType, mybir.AxisListType
    ADD, SUB, MUL = ALU.add, ALU.subtract, ALU.mult

    with ExitStack() as ctx:
        def sb(name, shape, dt=F32, where=ctx):
            return where.enter_context(nc.sbuf_tensor(name, shape, dt))

        def sem(name):
            return ctx.enter_context(nc.semaphore(name))

        h_hi = sb("h_hi", [P, KD, TOK], F32R)
        h_lo = sb("h_lo", [P, KD, TOK], F32R)
        x = sb("x", [P, KD, TOK])
        raw = sb("raw", [P, SLOTS, UNIT])
        w_hi = sb("w_hi", [P, SLOTS, UNIT], F32R)
        w_lo = sb("w_lo", [P, SLOTS, UNIT], F32R)
        act_t = sb("act_t", [P, 2, TOK])
        s_sum = sb("s_sum", [P, TOK])
        q_sum = sb("q_sum", [P, TOK])
        sq = sb("sq", [P, 2, TOK])
        var = sb("var", [P, TOK])
        y0 = sb("y0", [P, TOK])
        tmp = sb("tmp", [P, TOK])
        rstd = sb("rstd", [P, TOK])
        shift = sb("shift", [P, TOK])
        cols = sb("cols", [P, COLS])
        mod = sb("mod", [P, ADA])
        modb = sb("modb", [P, ADA])
        scale1 = sb("scale1", [P, 3, KD])
        G = sb("G", [P, 3, KD])
        B0 = sb("B0", [P, 3, KD])
        B = sb("B", [P, 3, KD])
        gate = sb("gate", [P, 3, KD])
        ag = sb("ag", [P, 3, KD])
        ab = sb("ab", [P, 3, KD])
        qg = sb("qg", [P, KQ])
        ones_t = sb("ones_t", [P, P])
        ones_d = sb("ones_d", [P, P])
        nmax = sb("nmax", [P, HEADS * QB])
        psums = sb("psums", [P, HEADS * QB])
        pinv = sb("pinv", [P, HEADS * QB])
        halfpi = sb("halfpi", [P, 1])
        unused = sb("unused", [P, 6])
        ident = cols[:, C_ID:C_ID + P]

        with ExitStack() as start:
            ada_first = sb("ada_first", [P, ADA_FIRST, D], F32, start)
        ffn_ctx = ExitStack()
        a_hi1 = sb("a_hi1", [P, FT, TOK], F32R, ffn_ctx)
        a_lo1 = sb("a_lo1", [P, FT, TOK], F32R, ffn_ctx)
        c_act = sb("c_act", [P, D], F32, ffn_ctx)
        ada_ring = sb("ada_ring", [P, 2, D], F32, ffn_ctx)
        ffn_ctx.close()
        mix_ctx = ExitStack()
        cqn_hi = sb("cqn_hi", [P, KQ, TOK], F32R, mix_ctx)
        cqn_lo = sb("cqn_lo", [P, KQ, TOK], F32R, mix_ctx)
        ckvn_hi = sb("ckvn_hi", [P, KKV, TOK], F32R, mix_ctx)
        ckvn_lo = sb("ckvn_lo", [P, KKV, TOK], F32R, mix_ctx)
        ckv = sb("ckv", [P, KKV, TOK], F32, mix_ctx)
        cq = sb("cq", [P, KQ, TOK], F32, mix_ctx)
        u = sb("u", [P, NPG, PADW + TOK], F32, mix_ctx)
        wsum = sb("wsum", [P, 2, PADW + TOK], F32, mix_ctx)
        Q = sb("Q", [P, HEADS, TOK], F32, mix_ctx)
        K = sb("K", [P, HEADS, TOK], F32, mix_ctx)
        V = sb("V", [P, QB, HEADS * VDIM], F32, mix_ctx)
        pt_even = sb("pt_even", [P, QB, TOK], F32, mix_ctx)
        poolw = sb("poolw", [P, NPG * P], F32, mix_ctx)
        mix_ctx.close()
        ffn_ctx = ExitStack()
        a_hi2 = sb("a_hi2", [P, FT, TOK], F32R, ffn_ctx)
        a_lo2 = sb("a_lo2", [P, FT, TOK], F32R, ffn_ctx)
        ffn_ctx.close()
        prob = cq
        PT = [pt_even[:, :, :], u[:, :, PADW:PADW + TOK]]
        kr = V[:, 1, :]
        rope_t = tmp
        pos_i = V[:, 0, :].bitcast(I32)
        ang, turns, k1, k2, r1, r2, r3 = (Q[:, j, :] for j in range(7))
        bank = [ctx.enter_context(nc.psum_tensor(f"bank{b}", [P, TOK], F32)) for b in range(8)]
        Y0, MEAN, SQR = 4, 6, 7

        s_cols, s_pos = sem("cols_loaded"), sem("pos_loaded")
        s_c, s_poolw = sem("c_loaded"), sem("poolw_loaded")
        s_x = [sem(f"x_loaded{i}") for i in range(2)]
        s_ada1 = [sem(f"ada_first_loaded{i}") for i in range(4)]
        s_raw = [sem(f"raw_loaded{i}") for i in range(SLOTS)]
        s_ada = [sem(f"ada_loaded{i}") for i in range(2)]
        s_adadone = sem("ada_tiles_done")
        s_cact = sem("c_act_ready")
        s_ones, s_pad = sem("ones_ready"), sem("pad_ready")
        s_hi, s_lo = sem("w_hi_done"), sem("w_lo_done")
        s_used = sem("units_used")
        s_col = sem("derived_columns")
        s_out = sem("out_stored")
        s_e = [sem(f"e_done{p}") for p in range(4)]
        s_sq = [sem(f"sq_done{p}") for p in range(4)]
        s_cm = [sem(f"tile0_mean{p}") for p in range(4)]
        s_cc = [sem(f"shift_copied{p}") for p in range(4)]
        s_xs = [sem(f"x_shifted{p}") for p in range(4)]
        s_acc = [sem(f"sums_done{p}") for p in range(4)]
        s_st = [sem(f"stats_done{p}") for p in range(4)]
        s_rq = [sem(f"root_act{p}") for p in range(4)]
        s_rv = [sem(f"root_dve{p}") for p in range(4)]
        s_nx = [sem(f"normal_steps{p}") for p in range(4)]
        s_hf = [sem(f"h_full{p}") for p in range(4)]
        s_hh = [sem(f"h_hi_done{p}") for p in range(4)]
        s_hl = [sem(f"h_lo_done{p}") for p in range(4)]
        s_res = [sem(f"residual_scaled{p}") for p in range(4)]
        s_silu = [sem(f"silu_done{f}") for f in range(2)]
        s_prod = [sem(f"product_done{f}") for f in range(2)]
        s_ah = [sem(f"a_hi_done{f}") for f in range(2)]
        s_al = [sem(f"a_lo_done{f}") for f in range(2)]
        s_grp = sem("mixer_groups")
        s_eva, s_evd = sem("evacuated_act"), sem("evacuated_dve")
        s_mst = sem("rms_sums")
        s_msum = sem("rms_partial")
        s_mv, s_ma = sem("rms_dve"), sem("rms_act")
        s_full = sem("lora_full")
        s_lh, s_ll = sem("lora_hi"), sem("lora_lo")
        s_rope, s_ropet = sem("rope_steps"), sem("rope_tables")
        s_krp = sem("k_rope_parts")
        s_kall = sem("k_rope_spread")
        s_qp, s_q = sem("q_rope_parts"), sem("q_ready")
        s_win = sem("window_sums")
        s_ph, s_pl = sem("pool_hi"), sem("pool_lo")
        s_s, s_mask, s_max = sem("scores_done"), sem("scores_masked"), sem("row_max_done")
        s_exp, s_inv, s_p = sem("exp_done"), sem("row_sum_inverse"), sem("probs_ready")
        s_t, s_te = sem("probs_transposed"), sem("pt_ready")
        s_pv, s_mh, s_ml = sem("pv_done"), sem("attn_hi"), sem("attn_lo")

        block = ctx.enter_context(nc.Block())

        T_KN = N_PROJ
        T_V = T_KN + HEADS // 2
        T_Q = T_V + QB
        T_PL = T_Q + HEADS
        T_END = T_PL + NPG
        BY = (["a"] * 2 + ["d"] + ["a"] * KQ + ["d"] * NPG + ["ad"] * (HEADS // 2) + ["a"] * QB
              + ["ad"] * HEADS + ["d"] * NPG)

        def emptied(eng, t):
            if "a" in BY[t]:
                eng.wait_ge(s_eva, sum("a" in b for b in BY[:t + 1]))
            if "d" in BY[t]:
                eng.wait_ge(s_evd, sum("d" in b for b in BY[:t + 1]))

        def group_ready(eng, t):
            if t < T_V:
                at = (s_grp, t - T_KN + 1) if t < T_V - 1 else (s_used, U_KNOPE + 1)
            elif t < T_Q:
                at = (s_grp, t - T_V + 4) if t < T_Q - 1 else (s_used, U_V + 1)
            elif t < T_PL:
                hd = t - T_Q
                at = (s_used, U_UQ + hd // 2 + 1) if hd % 2 else (s_grp, 7 + hd // 2)
            else:
                at = (s_grp, 7 + HEADS // 2 + t - T_PL)
            eng.wait_ge(*at)

        def attn_steps():
            n = HEADS * QB
            for k in range(n + 6):
                yield (k, k if k < n else None, k - 1 if 0 <= k - 1 < n else None,
                       k - 3 if 0 <= k - 3 < n else None,
                       (k - 4) // QB if (k - 4) % QB == QB - 1 and 0 <= k - 4 < n else None,
                       (k - 5) // QB if (k - 5) % QB == QB - 1 and 0 <= k - 5 < n else None)

        @block.sync
        def _(sp):
            for i in range(2):
                sp.dma_start(x[:, 4 * i:4 * i + 4, :],
                             xT[4 * i:4 * i + 4].rearrange("t p n -> p t n")).then_inc(s_x[i], 16)
            sp.dma_start(c_act[:], c_rows).then_inc(s_c, 16)
            sp.dma_start(cols[:], cols_dram).then_inc(s_cols, 16)

            def unit(f, i=0, lo=0, hi=1, j=None):
                n0 = f(i) if isinstance(i, int) else f(lo)
                slot = SLOT[n0]
                width = unit_width(n0)
                if PREV[n0] is not None:
                    sp.wait_ge(s_lo, affine(lambda k: PREV[f(k)] + 1, i, lo, hi))
                src = wunits[affine(f, i, lo, hi)] if isinstance(i, int) else \
                    wunits[bass.ds(affine(f, i, lo, hi), 1)].rearrange("a p n -> p (a n)")
                sp.dma_start(raw[:, slot, 0:width], src[:, 0:width]).then_inc(s_raw[slot], 16)

            def ada(f, i, lo, hi):
                s = (f(i) if isinstance(i, int) else f(lo)) % 2
                if not (isinstance(i, int) and f(i) < 2):
                    sp.wait_ge(s_adadone, affine(lambda k: ADA_FIRST + f(k) - 1, i, lo, hi))
                t = affine(lambda k: ADA_FIRST + f(k), i, lo, hi)
                src = ada_w[t] if isinstance(i, int) else \
                    ada_w[bass.ds(t, 1)].rearrange("a p n -> p (a n)")
                sp.dma_start(ada_ring[:, s, :], src).then_inc(s_ada[s], 16)

            for i in range(4):
                sp.dma_start(ada_first[:, 4 * i:4 * i + 4, :],
                             ada_w[4 * i:4 * i + 4].rearrange("t p n -> p t n")).then_inc(s_ada1[i], 16)
                unit(lambda k: i)
            for a in range(2):
                ada(lambda k: a, 0, 0, 1)

            def up_loads(base, i, lo, hi, with_ada):
                for ff in range(2):
                    for j in range(2):
                        unit(lambda k: base + 4 * k + 2 * ff + j + SLOTS, i, lo, hi)
                    if with_ada:
                        for j in range(2):
                            ada(lambda k: 4 * k + 2 * ff + j + 2, i, lo, hi)

            LASTB = FT // 2 - 1
            up_loads(F1, 0, 0, 1, True)
            with sp.Fori(1, LASTB) as i:
                up_loads(F1, i, 1, LASTB, True)
            up_loads(F1, LASTB, 0, 1, True)
            for m in range(KD - 1):
                for n in range(F1_DOWN + DPM * (m + 1) + 1, F1_DOWN + DPM * (m + 2) + 1):
                    unit(lambda k: n)
                for a in (2 * FT + 2 * m + 2, 2 * FT + 2 * m + 3):
                    if a < ADA - ADA_FIRST:
                        ada(lambda k: a, 0, 0, 1)
            for n in range(MX + 1, MX + SLOTS):
                unit(lambda k: n)
            sp.wait_ge(s_adadone, ADA)
            sp.wait_ge(s_used, MX)
            sp.dma_start(poolw[:], pool_w).then_inc(s_poolw, 16)
            sp.dma_start(pos_i, pos_rows).then_inc(s_pos, 16)
            for n in range(MX + SLOTS, F2 + SLOTS):
                unit(lambda k: n)
            with sp.Fori(0, LASTB) as i:
                up_loads(F2, i, 0, LASTB, False)
            up_loads(F2, LASTB, 0, 1, False)
            for n in range(F2 + UP + SLOTS, UNITS):
                unit(lambda k: n)
            for m in range(KD):
                sp.wait_ge(s_hh[3], m + 1)
                sp.dma_start(outT[m], x[:, m, :]).then_inc(s_out, 16)
            sp.wait_ge(s_out, 16 * KD)

        @block.tensor
        def _(pe):
            mm = nc.tensor.matmul

            def mm3(out, lhs, rhs, first, last):
                (lh, ll), (rh, rl) = lhs, rhs
                mm(out, lh, rh, start=first, stop=False)
                mm(out, lh, rl, start=False, stop=False)
                return mm(out, ll, rh, start=False, stop=last)

            def w(slot, col):
                return w_hi[:, slot, col:col + P], w_lo[:, slot, col:col + P]

            def h(k):
                return h_hi[:, k, :], h_lo[:, k, :]

            def first_units(base, p):
                for j in range(3):
                    pe.wait_ge(s_lo, base + j + 1)
                for k in range(KD):
                    pe.wait_ge(s_hh[p], k + 1)
                    for j in range(3):
                        wh, wl = w(SLOT[base + j], k * P)
                        mm(bank[j][:], wh, h_hi[:, k, :], start=k == 0, stop=False)
                        mm(bank[j][:], wl, h_hi[:, k, :], start=False, stop=False)
                    pe.wait_ge(s_hl[p], k + 1)
                    for j in range(3):
                        wh, _ = w(SLOT[base + j], k * P)
                        last = mm(bank[j][:], wh, h_lo[:, k, :], start=False, stop=k == KD - 1)
                        if k == KD - 1:
                            last.then_inc(s_used, 1)

            def whole_unit(n0, out):
                for k in range(KD):
                    last = mm3(out, w(SLOT[n0], k * P), h(k), k == 0, k == KD - 1)
                last.then_inc(s_used, 1)

            def up(base, ffn, i, lo, hi, units=range(4)):
                for j in units:
                    pe.wait_ge(s_lo, affine(lambda k: base + 4 * k + j + 1, i, lo, hi))
                    if j % 2 == 0 and not (isinstance(i, int) and i == 0):
                        pe.wait_ge(s_prod[ffn], affine(lambda k: 2 * k + j // 2 - 1, i, lo, hi))
                    whole_unit(base + 4 * lo + j, bank[j][:])

            def shift_mean(p):
                pe.wait_ge(s_e[p], 1)
                mm(bank[MEAN][:], ones_t[:], x[:, 0, :], start=True, stop=True).then_inc(s_cm[p], 1)

            def stats_begin(p):
                pe.wait_ge(s_acc[p], 2 * (KD - 2))
                mm(bank[MEAN][:], ones_d[:], s_sum[:], start=True, stop=False)
                mm(bank[SQR][:], ones_d[:], q_sum[:], start=True, stop=False)

            def stats_end(p):
                pe.wait_ge(s_e[p], KD)
                mm(bank[MEAN][:], ones_d[:], x[:, KD - 1, :], start=False, stop=True).then_inc(s_st[p], 1)
                pe.wait_ge(s_sq[p], KD)
                mm(bank[SQR][:], ones_d[:], sq[:, (KD - 1) % 2, :], start=False, stop=True)\
                    .then_inc(s_st[p], 1)

            def down_tile(base, per, p, rhs, k_last, i, lo, hi, par, m0=None, ready=None):
                y = bank[Y0 + par][:]
                for j in range(per):
                    pe.wait_ge(s_lo, affine(lambda k: base + per * (2 * k + par) + j + 1, i, lo, hi))
                    if j == 0 and (m0 is None or m0 >= 2):
                        pe.wait_ge(s_e[p], affine(lambda k: 2 * k + par - 1, i, lo, hi))
                    slot = SLOT[base + per * (2 * lo + par) + j]
                    for kk in range(k_last if j == per - 1 else KD):
                        k = KD * j + kk
                        if m0 == 0 and ready is not None and ready(k) is not None:
                            pe.wait_ge(*ready(k))
                        if m0 == 1 and k == (4 if per == 1 else KD):
                            shift_mean(p)
                        if m0 == KD - 1 and k == KD * (per - 1) + 4:
                            stats_begin(p)
                        last = mm3(y, w(slot, kk * P), rhs(k), k == 0,
                                   j == per - 1 and kk == k_last - 1)
                    last.then_inc(s_used, 1)

            def down(base, per, p, rhs, k_last, ready, loop):
                for m in range(2):
                    down_tile(base, per, p, rhs, k_last, 0, 0, 1, m, m, ready)
                if loop:
                    with pe.Fori(1, KD // 2 - 1) as i:
                        for par in range(2):
                            down_tile(base, per, p, rhs, k_last, i, 1, KD // 2 - 1, par)
                else:
                    for m in range(2, KD - 2):
                        down_tile(base, per, p, rhs, k_last, m // 2, m // 2, 0, m % 2, m)
                for m in range(KD - 2, KD):
                    down_tile(base, per, p, rhs, k_last, m // 2, m // 2, 0, m % 2, m)
                stats_end(p)

            def ffn(base, f, p, a_hi, a_lo):
                first_units(base, p)
                up(base, f, 0, 0, 1, units=(3,))
                with pe.Fori(1, FT // 2) as i:
                    up(base, f, i, 1, FT // 2)

                def ready(k):
                    if k % 8 == 0 and k < 16:
                        return s_al[f], k + 8
                    return (s_al[f], k + 1) if k >= 16 else None
                down(base + UP, DPM, p + 1, lambda k: (a_hi[:, k, :], a_lo[:, k, :]), LAST_K,
                     ready, True)

            pe.wait_ge(s_ones, 2)
            pe.wait_ge(s_x[0], 16)
            mm(bank[MEAN][:], ones_t[:], x[:, 0, :], start=True, stop=True).then_inc(s_cm[0], 1)
            pe.wait_ge(s_cc[0], 1)
            for m in range(KD):
                pe.wait_ge(s_e[0], m + 1)
                mm(bank[MEAN][:], ones_d[:], x[:, m, :], start=m == 0, stop=m == KD - 1)
                pe.wait_ge(s_sq[0], m + 1)
                mm(bank[SQR][:], ones_d[:], sq[:, m % 2, :], start=m == 0, stop=m == KD - 1)\
                    .then_inc(s_st[0], 1)

            ffn(F1, 0, 0, a_hi1, a_lo1)

            first_units(MX, 1)
            for t in range(3, N_PROJ):
                pe.wait_ge(s_lo, MX + t + 1)
                if t >= 4:
                    emptied(pe, t - 4)
                whole_unit(MX + t, bank[t % 4][:])
                if t == 4:
                    pe.wait_ge(s_msum, 1)
                    mm(bank[MEAN][:], ones_t[:], s_sum[:], start=True, stop=True).then_inc(s_mst, 1)
                if t == 7:
                    pe.wait_ge(s_msum, KQ)
                    mm(bank[SQR][:], ones_t[:], q_sum[:], start=True, stop=True).then_inc(s_mst, 1)
            pe.wait_ge(s_lo, U_KNOPE + 1)
            pe.wait_ge(s_ll, KKV)
            for j in range(HEADS // 2):
                t = T_KN + j
                emptied(pe, t - 4)
                for k in range(KKV):
                    last = mm3(bank[t % 4][:], w(SLOT[U_KNOPE], (k * 4 + j) * P),
                               (ckvn_hi[:, k, :], ckvn_lo[:, k, :]), k == 0, k == KKV - 1)
                last.then_inc(s_used if j == HEADS // 2 - 1 else s_grp, 1)
            pe.wait_ge(s_lo, U_V + 1)
            for j in range(QB):
                t = T_V + j
                emptied(pe, t - 4)
                for k in range(KKV):
                    sl, c0 = SLOT[U_V], k * HEADS * VDIM
                    last = mm3(bank[t % 4][:],
                               (ckvn_hi[:, k, j * P:(j + 1) * P], ckvn_lo[:, k, j * P:(j + 1) * P]),
                               (w_hi[:, sl, c0:c0 + HEADS * VDIM], w_lo[:, sl, c0:c0 + HEADS * VDIM]),
                               k == 0, k == KKV - 1)
                last.then_inc(s_used if j == QB - 1 else s_grp, 1)
            for hd in range(HEADS):
                t = T_Q + hd
                pe.wait_ge(s_lo, U_UQ + hd // 2 + 1)
                pe.wait_ge(s_ll, KKV + KQ)
                emptied(pe, t - 4)
                for k in range(KQ):
                    last = mm3(bank[t % 4][:], w(SLOT[U_UQ + hd // 2], (hd % 2 * KQ + k) * P),
                               (cqn_hi[:, k, :], cqn_lo[:, k, :]), k == 0, k == KQ - 1)
                last.then_inc(s_used if hd % 2 else s_grp, 1)
            pe.wait_ge(s_poolw, 16)
            for g in range(NPG):
                t = T_PL + g
                emptied(pe, t - 4)
                pe.wait_ge(s_win, POOLED[g])
                mm(bank[t % 4][:], poolw[:, g * P:(g + 1) * P], u[:, g, PADW:], start=True, stop=True)\
                    .then_inc(s_grp, 1)
            pe.wait_ge(s_kall, 1)
            pe.wait_ge(s_eva, sum("a" in b for b in BY))
            for step, k, _, kt, hv, _ in attn_steps():
                if k is not None:
                    hd, i = divmod(k, QB)
                    pe.wait_ge(s_q, hd + 1)
                    if k >= 3:
                        pe.wait_ge(s_exp, k - 2)
                    mm(bank[4 + k % 3][:, 0:(i + 1) * P], Q[0:NOPE + ROPE, hd, i * P:(i + 1) * P],
                       K[0:NOPE + ROPE, hd, 0:(i + 1) * P], start=True, stop=True).then_inc(s_s, 1)
                if kt is not None:
                    hd, i = divmod(kt, QB)
                    if kt == 0:
                        pe.wait_ge(s_evd, sum("d" in b for b in BY))
                    pe.wait_ge(s_p, kt + 1)
                    if kt >= 2:
                        pe.wait_ge(s_te, kt - 1)
                    out = bank[7 if kt % 2 == 0 else 3]
                    for j in range(i + 1):
                        last = nc.tensor.transpose(out[:, j * P:(j + 1) * P],
                                                   prob[:, kt % 3, j * P:(j + 1) * P], ident)
                    last.then_inc(s_t, 1)
                if hv is not None:
                    pe.wait_ge(s_te, QB * (hv + 1))
                    if hv >= 4:
                        pe.wait_ge(s_ml, hv - 3)
                    r0 = VDIM * (hv % 2)
                    for j in range(QB):
                        last = mm(bank[hv // 2 % 2][r0:r0 + VDIM, j * P:],
                                  V[:, j, hv * VDIM:(hv + 1) * VDIM], PT[hv % 2][:, j, j * P:],
                                  start=j == 0, stop=j == QB - 1)
                    last.then_inc(s_pv, 1)
            down(U_OUT, 1, 2, h, KD,
                 lambda k: {0: (s_ml, HEADS), HEADS // 2: (s_pl, NPG)}.get(k), False)

            ffn(F2, 1, 2, a_hi2, a_lo2)

        def act_hi(act, f, i=0, lo=0, hi=1):
            n0 = f(i) if isinstance(i, int) else f(lo)
            act.wait_ge(s_raw[SLOT[n0]], affine(lambda k: 16 * FILL[f(k)], i, lo, hi))
            if PREV[n0] is not None:
                act.wait_ge(s_used, affine(lambda k: PREV[f(k)] + 1, i, lo, hi))
            w_ = unit_width(n0)
            nc.scalar.activation(w_hi[:, SLOT[n0], 0:w_], raw[:, SLOT[n0], 0:w_], ACT.Copy)\
                .then_inc(s_hi, 1)

        def dve_lo(dve, f, i=0, lo=0, hi=1):
            n0 = f(i) if isinstance(i, int) else f(lo)
            dve.wait_ge(s_hi, affine(lambda k: f(k) + 1, i, lo, hi))
            w_ = unit_width(n0)
            nc.vector.tensor_tensor(w_lo[:, SLOT[n0], 0:w_], raw[:, SLOT[n0], 0:w_],
                                    w_hi[:, SLOT[n0], 0:w_].bitcast(F32), SUB).then_inc(s_lo, 1)

        @block.scalar
        def _(act):
            fn = nc.scalar.activation

            def root(p, mean_at):
                act.wait_ge(s_st[p], mean_at)
                fn(tmp[:], bank[MEAN][:], ACT.Square).then_inc(s_rq[p], 1)
                act.wait_ge(s_rv[p], 1)
                fn(y0[:], var[:], ACT.Ln).then_inc(s_rq[p], 1)
                act.wait_ge(s_rq[p], 2)
                fn(y0[:], y0[:], ACT.Exp, scale=-0.5).then_inc(s_rq[p], 1)

            def preload(n, func):
                act.wait_ge(s_ones, 3)
                fn(unused[:, n:n + 1], halfpi[:], func)

            def h_split(p):
                for m in range(KD):
                    act.wait_ge(s_hf[p], m + 1)
                    fn(h_hi[:, m, :], act_t[:, m % 2, :], ACT.Copy).then_inc(s_hh[p], 1)

            def square(p, m):
                if m == 0:
                    return
                if m == 1:
                    act.wait_ge(s_xs[p], 1)
                    fn(q_sum[:], x[:, 0, :], ACT.Square).then_inc(s_sq[p], 1)
                act.wait_ge(s_e[p], m + 1)
                if m >= 3:
                    act.wait_ge(s_acc[p], 2 * (m - 2))
                fn(sq[:, m % 2, :], x[:, m, :], ACT.Square).then_inc(s_sq[p], 1)

            def up(base, f, a_hi, i, lo, hi):
                for ff in range(2):
                    act.wait_ge(s_used, affine(lambda k: base + 4 * k + 2 * ff + 1, i, lo, hi))
                    if not (isinstance(i, int) and i == 0):
                        act.wait_ge(s_al[f], affine(lambda k: 2 * k + ff - 1, i, lo, hi))
                    fn(act_t[:, ff, :], bank[2 * ff][:], ACT.Silu).then_inc(s_silu[f], 1)
                    for j in range(2):
                        if isinstance(i, int) and base + 4 * i + 2 * ff + j + SLOTS >= base + UP + DPM:
                            continue
                        act_hi(act, lambda k: base + 4 * k + 2 * ff + j + SLOTS, i, lo, hi)
                    act.wait_ge(s_prod[f], affine(lambda k: 2 * k + ff + 1, i, lo, hi))
                    t = affine(lambda k: 2 * k + ff, i, lo, hi)
                    dst = a_hi[:, t, :] if isinstance(i, int) else \
                        a_hi[:, bass.ds(t, 1), :].rearrange("p a n -> p (a n)")
                    fn(dst, act_t[:, ff, :], ACT.Copy).then_inc(s_ah[f], 1)

            def ffn(base, f, p, a_hi):
                up(base, f, a_hi, 0, 0, 1)
                with act.Fori(1, FT // 2 - 1) as i:
                    up(base, f, a_hi, i, 1, FT // 2 - 1)
                up(base, f, a_hi, FT // 2 - 1, 0, 1)
                for m in range(KD):
                    units = [base + UP + DPM * (m + 1) + j for j in range(DPM)]
                    for j, n in enumerate(units):
                        if j == DPM - 1 and m < KD - 1:
                            square(p, m)
                        if n < UNITS:
                            act_hi(act, lambda k: n)
                preload(2 + f, ACT.Ln)
                square(p, KD - 1)
                root(p, 1)

            act.wait_ge(s_c, 16)
            fn(c_act[:], c_act[:], ACT.Silu).then_inc(s_cact, 1)
            preload(0, ACT.Ln)
            for m in range(KD):
                act.wait_ge(s_e[0], m + 1)
                if m >= 2:
                    act.wait_ge(s_st[0], m - 1)
                fn(sq[:, m % 2, :], x[:, m, :], ACT.Square).then_inc(s_sq[0], 1)
            root(0, KD)
            for n in range(SLOTS):
                act_hi(act, lambda k: n)
            preload(1, ACT.Silu)
            h_split(0)
            ffn(F1, 0, 1, a_hi1)
            h_split(1)

            act_hi(act, lambda k: MX + 3)

            def latent(t, dst, sq_dst):
                act.wait_ge(s_used, MX + t + 1)
                fn(dst, bank[t % 4][:], ACT.Copy)
                fn(sq_dst, bank[t % 4][:], ACT.Square).then_inc(s_eva, 1)
                act_hi(act, lambda k: MX + t + SLOTS)

            def rms_root(which):
                act.wait_ge(s_mv, 4 * which + 1)
                fn(y0[:], var[:], ACT.Ln).then_inc(s_ma, 1)
                act.wait_ge(s_ma, 2 * which + 1)
                fn(y0[:], y0[:], ACT.Exp, scale=-0.5).then_inc(s_ma, 1)

            latent(0, ckv[:, 0, :], s_sum[:])
            latent(1, ckv[:, 1, :], sq[:, 0, :])
            act_hi(act, lambda k: MX + 2 + SLOTS)
            latent(3, cq[:, 0, :], q_sum[:])
            latent(4, cq[:, 1, :], sq[:, 1, :])
            rms_root(0)
            act.wait_ge(s_msum, 1)
            latent(5, cq[:, 2, :], sq[:, 0, :])
            for j in range(KKV):
                act.wait_ge(s_full, j + 1)
                fn(ckvn_hi[:, j, :], ckv[:, j, :], ACT.Copy).then_inc(s_lh, 1)
            act.wait_ge(s_msum, 2)
            latent(6, cq[:, 3, :], sq[:, 1, :])
            act_hi(act, lambda k: MX + 7 + SLOTS)
            rms_root(1)
            for j in range(KQ):
                act.wait_ge(s_full, KKV + j + 1)
                fn(cqn_hi[:, j, :], cq[:, j, :], ACT.Copy).then_inc(s_lh, 1)
            act_hi(act, lambda k: MX + 8 + SLOTS)
            act_hi(act, lambda k: MX + 9 + SLOTS)
            act_hi(act, lambda k: MX + 10 + SLOTS)
            for j in range(HEADS // 2):
                t = T_KN + j
                group_ready(act, t)
                fn(K[0:NOPE, 2 * j, :], bank[t % 4][0:NOPE, :], ACT.Copy).then_inc(s_eva, 1)
            act_hi(act, lambda k: U_KNOPE + SLOTS)
            act.wait_ge(s_rope, ROPE_STEPS)
            fn(rope_t[64:96, :], r1[64:96, :], ACT.Abs).then_inc(s_ropet, 1)
            act.wait_ge(s_ropet, 1)
            act.wait_ge(s_cols, 16)
            fn(rope_t[64:96, :], rope_t[64:96, :], ACT.Sin, scale=-1.0,
               bias=halfpi[64:96, :]).then_inc(s_ropet, 1)
            fn(rope_t[96:128, :], r1[96:128, :], ACT.Sin,
               scale=cols[96:128, C_SIGN:C_SIGN + 1]).then_inc(s_ropet, 1)
            for j in range(QB):
                t = T_V + j
                if j == 0:
                    act.wait_ge(s_krp, 3)
                group_ready(act, t)
                fn(V[:, j, :], bank[t % 4][:], ACT.Copy).then_inc(s_eva, 1)
            act_hi(act, lambda k: U_V + SLOTS)
            fn(K[64:96, :, :], act_t[64:96, 1:2, :].to_broadcast([32, HEADS, TOK]), ACT.Copy)\
                .then_inc(s_kall, 1)
            for hd in range(HEADS):
                t = T_Q + hd
                group_ready(act, t)
                fn(Q[0:NOPE, hd, :], bank[t % 4][0:NOPE, :], ACT.Copy).then_inc(s_eva, 1)
                if hd % 2:
                    act_hi(act, lambda k: U_UQ + hd // 2 + SLOTS)
            for g in range(NPG):
                act.wait_ge(s_evd, sum("d" in b for b in BY[:T_PL + g + 1]))
                fn(h_hi[:, HEADS // 2 + g, :], act_t[:, g % 2, :], ACT.Copy).then_inc(s_ph, 1)
            for step, k, _, kt, _, hm in attn_steps():
                if k is not None:
                    i = k % QB
                    act.wait_ge(s_max, k + 1)
                    if k >= 3:
                        act.wait_ge(s_t, k - 2)
                    fn(prob[:, k % 3, 0:(i + 1) * P], bank[4 + k % 3][:, 0:(i + 1) * P], ACT.Exp,
                       bias=nmax[:, k:k + 1], accum_out=psums[:, k:k + 1]).then_inc(s_exp, 1)
                if kt is not None:
                    hd, i = divmod(kt, QB)
                    act.wait_ge(s_t, kt + 1)
                    if i == 0 and hd >= 2:
                        act.wait_ge(s_pv, hd - 1)
                    fn(PT[hd % 2][:, 0:i + 1, i * P:(i + 1) * P],
                       bank[7 if kt % 2 == 0 else 3][:, 0:(i + 1) * P]
                       .rearrange("p (j n) -> p j n", n=P), ACT.Copy).then_inc(s_te, 1)
                if hm is not None:
                    act.wait_ge(s_pv, hm + 1)
                    r0 = VDIM * (hm % 2)
                    fn(h_hi[r0:r0 + VDIM, hm // 2, :], bank[hm // 2 % 2][r0:r0 + VDIM, :],
                       ACT.Copy).then_inc(s_mh, 1)
            for m in range(KD):
                if m < KD - 1:
                    act_hi(act, lambda k: U_OUT + m + SLOTS)
                if m == KD - 1:
                    preload(4, ACT.Ln)
                square(2, m)
            root(2, 1)
            preload(5, ACT.Silu)
            h_split(2)
            act_hi(act, lambda k: F2 + 3)
            ffn(F2, 1, 3, a_hi2)
            for m in range(KD):
                act.wait_ge(s_nx[3], 2 * m + 2)
                fn(x[:, m, :], x[:, m, :], ACT.Identity, scale=cols[:, C_LNG + 3 * KD + m:C_LNG + 3 * KD + m + 1],
                   bias=cols[:, C_LNB + 3 * KD + m:C_LNB + 3 * KD + m + 1]).then_inc(s_hh[3], 1)

        @block.vector
        def _(dve):
            tt, ts, stt, cp = (nc.vector.tensor_tensor, nc.vector.tensor_scalar,
                               nc.vector.scalar_tensor_tensor, nc.vector.tensor_copy)

            junk_start, junk_ring = act_t[:, 0, :].bitcast(BF16), var[:].bitcast(BF16)

            def ada(slot_ap, loaded, t, prev_done, junk=junk_ring):
                dve.wait_ge(*loaded)
                if prev_done is not None:
                    dve.wait_ge(s_adadone, prev_done)
                dst = mod[:, t:t + 1] if isinstance(t, int) else mod[:, bass.ds(t, 1)]
                stt(junk, slot_ap, 1.0, c_act[:], MUL, MUL, accum_out=dst)\
                    .then_inc(s_adadone, 1)

            def ada_ring_tile(f, i, lo, hi):
                a0 = f(i) if isinstance(i, int) else f(lo)
                ada(ada_ring[:, a0 % 2, :],
                    (s_ada[a0 % 2], affine(lambda k: 16 * (f(k) // 2 + 1), i, lo, hi)),
                    affine(lambda k: ADA_FIRST + f(k), i, lo, hi),
                    affine(lambda k: ADA_FIRST + f(k), i, lo, hi))

            ncol = [0]

            def col(ins):
                ins.then_inc(s_col, 1)
                ncol[0] += 1
                dve.wait_ge(s_col, ncol[0])

            def c8(c):
                return cols[:, c:c + KD]

            def add_bias(a, b):
                col(tt(modb[:, a:b], mod[:, a:b], cols[:, C_BADA + a:C_BADA + b], ADD))

            def derive_in(s):
                sh, sc = 3 * KD * s, 3 * KD * s + KD
                add_bias(sh, sh + 2 * KD)
                col(ts(scale1[:, s, :], modb[:, sc:sc + KD], 1.0, None, ADD))
                col(tt(G[:, s, :], scale1[:, s, :], c8(C_LNG + s * KD), MUL))
                col(tt(B0[:, s, :], scale1[:, s, :], c8(C_LNB + s * KD), MUL))
                col(tt(B[:, s, :], B0[:, s, :], modb[:, sh:sh + KD], ADD))
                col(ts(ag[:, s, :], c8(C_LNG + s * KD), ALPHA, None, MUL))
                col(ts(ab[:, s, :], c8(C_LNB + s * KD), ALPHA, None, MUL))

            def derive_gate(s):
                g = 3 * KD * s + 2 * KD
                add_bias(g, g + KD)
                col(ts(gate[:, s, :], modb[:, g:g + KD], 1.0 if s == 1 else 0.5, None, MUL))

            def root(p, both_at):
                dve.wait_ge(s_st[p], both_at)
                dve.wait_ge(s_rq[p], 1)
                stt(var[:], bank[SQR][:], LN_EPS, tmp[:], ADD, SUB).then_inc(s_rv[p], 1)
                dve.wait_ge(s_rq[p], 3)
                tt(tmp[:], y0[:], y0[:], MUL).then_inc(s_rv[p], 1)
                dve.wait_ge(s_rv[p], 2)
                stt(tmp[:], tmp[:], -0.5, var[:], MUL, MUL).then_inc(s_rv[p], 1)
                dve.wait_ge(s_rv[p], 3)
                stt(rstd[:], tmp[:], 1.5, y0[:], ADD, MUL).then_inc(s_rv[p], 1)
                dve.wait_ge(s_rv[p], 4)
                stt(shift[:], bank[MEAN][:], -1.0, rstd[:], MUL, MUL).then_inc(s_rv[p], 1)

            def h_full(p, m):
                dve.wait_ge(s_nx[p], 2 * m + 2)
                if m >= 2:
                    dve.wait_ge(s_hl[p], m - 1)
                ts(act_t[:, m % 2, :], x[:, m, :], G[:, p, m:m + 1], B[:, p, m:m + 1], MUL, ADD)\
                    .then_inc(s_hf[p], 1)

            def normalise(p, h_too=True):
                dve.wait_ge(s_rv[p], 4)

                def a(m):
                    tt(x[:, m, :], x[:, m, :], rstd[:], MUL).then_inc(s_nx[p], 1)

                def b(m):
                    if m == 0:
                        dve.wait_ge(s_rv[p], 5)
                    dve.wait_ge(s_nx[p], 2 * m + 1)
                    tt(x[:, m, :], x[:, m, :], shift[:], ADD).then_inc(s_nx[p], 1)

                a(0)
                for m in range(KD):
                    b(m)
                    if m + 1 < KD:
                        a(m + 1)
                    if h_too:
                        h_full(p, m)

            def residual(p, m, ready_at):
                if m == 0:
                    dve.wait_ge(s_res[p - 1], KD)
                dve.wait_ge(s_used, ready_at)
                if m == 1:
                    dve.wait_ge(s_cm[p], 1)
                    cp(shift[:], bank[MEAN][:]).then_inc(s_cc[p], 1)
                if m >= 1:
                    dve.wait_ge(s_xs[p], m + 1)
                stt(x[:, m, :], bank[Y0 + m % 2][:], gate[:, p - 1, m:m + 1], x[:, m, :], MUL, ADD)\
                    .then_inc(s_e[p], 1)

            def up(base, f, with_ada, i, lo, hi):
                for ff in range(2):
                    for j in range(2):
                        if with_ada and j == 0:
                            ada_ring_tile(lambda k: 4 * k + 2 * ff, i, lo, hi)
                        skip = isinstance(i, int) and 4 * i + 2 * ff + j + SLOTS >= UP + DPM
                        if not skip:
                            dve_lo(dve, lambda k: base + 4 * k + 2 * ff + j + SLOTS, i, lo, hi)
                        if j == 0:
                            dve.wait_ge(s_silu[f], affine(lambda k: 2 * k + ff + 1, i, lo, hi))
                            dve.wait_ge(s_used, affine(lambda k: base + 4 * k + 2 * ff + 2, i, lo, hi))
                            tt(act_t[:, ff, :], act_t[:, ff, :], bank[2 * ff + 1][:], MUL)\
                                .then_inc(s_prod[f], 1)
                    if with_ada:
                        ada_ring_tile(lambda k: 4 * k + 2 * ff + 1, i, lo, hi)

            def ffn(base, f, p):
                up(base, f, f == 0, 0, 0, 1)
                with dve.Fori(1, FT // 2 - 1) as i:
                    up(base, f, f == 0, i, 1, FT // 2 - 1)
                up(base, f, f == 0, FT // 2 - 1, 0, 1)
                if f == 0:
                    dve.wait_ge(s_adadone, ADA_FIRST + 2 * FT)
                    derive_gate(0)
                    derive_in(1)
                    derive_gate(1)
                for m in range(KD):
                    for j in range(DPM):
                        n = base + UP + DPM * (m + 1) + j
                        if j == DPM - 1 and m < KD - 1:
                            residual(p, m, base + UP + DPM * (m + 1))
                        if n < UNITS:
                            dve_lo(dve, lambda k: n)
                        a = 2 * FT + 2 * m + j
                        if f == 0 and j < 2 and a < ADA - ADA_FIRST:
                            ada_ring_tile(lambda k: a, 0, 0, 1)
                    if f == 0 and m == KD - 2:
                        dve.wait_ge(s_adadone, ADA)
                        derive_in(2)
                        derive_gate(2)
                residual(p, KD - 1, base + UP + DPM * KD)
                root(p, 2)
                normalise(p, h_too=p < 3)

            dve.wait_ge(s_cm[0], 1)
            cp(shift[:], bank[MEAN][:]).then_inc(s_cc[0], 1)
            dve.wait_ge(s_cc[0], 1)
            for m in range(KD):
                if m % 4 == 0:
                    dve.wait_ge(s_x[m // 4], 16)
                tt(x[:, m, :], x[:, m, :], shift[:], SUB).then_inc(s_e[0], 1)
            dve.wait_ge(s_cact, 1)
            for t in range(ADA_FIRST // 2):
                ada(ada_first[:, t, :], (s_ada1[t // 4], 16), t, t if t else None,
                    junk_start)
            root(0, KD)
            normalise(0, h_too=False)
            for t in range(ADA_FIRST // 2, ADA_FIRST):
                ada(ada_first[:, t, :], (s_ada1[t // 4], 16), t, t, junk_start)
                if t % 2:
                    dve_lo(dve, lambda k: (t - ADA_FIRST // 2) // 2)
            dve.wait_ge(s_adadone, ADA_FIRST)
            dve.wait_ge(s_cols, 16)
            derive_in(0)
            col(ts(qg[:], cols[:, C_QG:C_QG + KQ], SM_SCALE, None, MUL))
            for m in range(KD):
                h_full(0, m)
            ffn(F1, 0, 1)

            def lo_after(n):
                dve_lo(dve, lambda k: n + SLOTS)

            def rms_newton(which, src, scale):
                dve.wait_ge(s_mst, which + 1)
                b = 4 * which
                ts(var[:], src, scale, RMS_EPS, MUL, ADD).then_inc(s_mv, 1)
                dve.wait_ge(s_ma, 2 * which + 2)
                tt(tmp[:], y0[:], y0[:], MUL).then_inc(s_mv, 1)
                dve.wait_ge(s_mv, b + 2)
                stt(tmp[:], tmp[:], -0.5, var[:], MUL, MUL).then_inc(s_mv, 1)
                dve.wait_ge(s_mv, b + 3)
                stt(rstd[:], tmp[:], 1.5, y0[:], ADD, MUL).then_inc(s_mv, 1)
                dve.wait_ge(s_mv, b + 4)

            def u_out(g):
                dve.wait_ge(s_used, MX + 3 + KQ + g + 1)
                cp(u[:, g, PADW:], bank[(3 + KQ + g) % 4][:]).then_inc(s_evd, 1)

            nrope = [0]

            def rp(ins):
                ins.then_inc(s_rope, 1)
                nrope[0] += 1
                dve.wait_ge(s_rope, nrope[0])

            def nearest(dst, src, scale):
                rp(ts(dst, src, scale, MAGIC, MUL, ADD))
                rp(ts(dst, dst, -MAGIC, None, ADD))

            def reduce_angle(r):
                nearest(turns, r, 1.0 / (2.0 * math.pi))
                for part in TWO_PI_PARTS:
                    rp(stt(r, turns, -part, r, MUL, ADD))

            def rope_angles():
                dve.wait_ge(s_pos, 16)
                rp(cp(ang, pos_i))
                rp(ts(ang, ang, cols[:, C_FREQ:C_FREQ + 1], None, MUL))
                nearest(k1, ang, 2.0 ** -12)
                rp(stt(r1, k1, -2.0 ** 12, ang, MUL, ADD))
                nearest(k2, k1, 2.0 ** -10)
                rp(stt(k1, k2, -2.0 ** 10, k1, MUL, ADD))

            def rope_high_parts():
                rp(ts(r2, k1, PI12_PARTS[0], None, MUL))
                reduce_angle(r2)
                rp(stt(r2, k1, PI12_PARTS[1], r2, MUL, ADD))
                rp(ts(r3, k2, PI22_PARTS[0], None, MUL))
                reduce_angle(r3)
                rp(stt(r3, k2, PI22_PARTS[1], r3, MUL, ADD))

            def rope_sum():
                rp(tt(r1, r1, r2, ADD))
                rp(tt(r1, r1, r3, ADD))
                reduce_angle(r1)
                rp(ts(r1, r1, PI_CLAMP, -PI_CLAMP, ALU.min, ALU.max))

            dve_lo(dve, lambda k: MX + 3)
            lo_after(MX)
            lo_after(MX + 1)
            dve.wait_ge(s_used, MX + 3)
            dve.wait_ge(s_pos, 16)
            cp(kr[64:128, :], bank[2][64:128, :]).then_inc(s_evd, 1)
            lo_after(MX + 2)
            rope_angles()
            lo_after(MX + 3)
            lo_after(MX + 4)
            rms_newton(0, bank[MEAN][:], P / KVR)
            for j in range(KKV):
                stt(ckv[:, j, :], ckv[:, j, :], cols[:, C_KVG + j:C_KVG + j + 1], rstd[:], MUL, MUL)\
                    .then_inc(s_full, 1)
            lo_after(MX + 5)
            reduce_angle(r1)
            rope_high_parts()
            lo_after(MX + 6)
            u_out(0)
            rope_sum()
            assert nrope[0] == ROPE_STEPS
            lo_after(MX + 7)
            rms_newton(1, bank[SQR][:], P / QR)
            for j in range(KQ):
                stt(cq[:, j, :], cq[:, j, :], qg[:, j:j + 1], rstd[:], MUL, MUL).then_inc(s_full, 1)
            u_out(1)
            lo_after(MX + 8)
            u_out(2)
            lo_after(MX + 9)
            u_out(3)
            lo_after(MX + 10)
            for j in range(HEADS // 2):
                t = T_KN + j
                group_ready(dve, t)
                cp(K[0:NOPE, 2 * j + 1, :], bank[t % 4][NOPE:2 * NOPE, :]).then_inc(s_evd, 1)
            lo_after(U_KNOPE)
            dve.wait_ge(s_ropet, 3)
            tt(kr[64:128, :], kr[64:128, :], rope_t[64:128, :], MUL).then_inc(s_krp, 1)
            dve.wait_ge(s_krp, 1)
            cp(act_t[64:96, 0, :], kr[96:128, :]).then_inc(s_krp, 1)
            dve.wait_ge(s_krp, 2)
            tt(act_t[64:96, 1, :], act_t[64:96, 0, :], kr[64:96, :], ADD).then_inc(s_krp, 1)
            lo_after(U_V)
            for hd in range(HEADS):
                t = T_Q + hd
                b = bank[t % 4]
                group_ready(dve, t)
                if hd == 0:
                    dve.wait_ge(s_kall, 1)
                if hd >= 2:
                    dve.wait_ge(s_q, hd - 1)
                tt(Q[64:96, hd, :], b[64:96, :], rope_t[64:96, :], MUL).then_inc(s_qp, 1)
                tt(act_t[64:96, hd % 2, :], b[96:128, :], rope_t[96:128, :], MUL).then_inc(s_evd, 1)
                if hd % 2:
                    lo_after(U_UQ + hd // 2)
            for g in range(NPG):
                t = T_PL + g
                group_ready(dve, t)
                if g < 2:
                    dve.wait_ge(s_q, HEADS)
                else:
                    dve.wait_ge(s_pl, g - 1)
                ts(act_t[:, g % 2, :], bank[t % 4][:], cols[:, C_PB + g:C_PB + g + 1],
                   cols[:, C_PS + g:C_PS + g + 1], ADD, MUL).then_inc(s_evd, 1)
            for step, k, kn, _, _, hm in attn_steps():
                if k is not None:
                    i = k % QB
                    b = bank[4 + k % 3]
                    dve.wait_ge(s_s, k + 1)
                    nc.vector.memset(b[0:CHUNK, i * P + CHUNK:(i + 1) * P], MASKED).then_inc(s_mask, 1)
                    dve.wait_ge(s_mask, k + 1)
                    nc.vector.reduce_max(nmax[:, k:k + 1], b[:, 0:(i + 1) * P], AX.X, negate=True)\
                        .then_inc(s_max, 1)
                if kn is not None:
                    i = kn % QB
                    dve.wait_ge(s_exp, kn + 1)
                    nc.vector.reciprocal(pinv[:, kn:kn + 1], psums[:, kn:kn + 1]).then_inc(s_inv, 1)
                    dve.wait_ge(s_inv, kn + 1)
                    pr = prob[:, kn % 3, 0:(i + 1) * P]
                    ts(pr, pr, pinv[:, kn:kn + 1], None, MUL).then_inc(s_p, 1)
                if hm is not None:
                    dve.wait_ge(s_mh, hm + 1)
                    r0 = VDIM * (hm % 2)
                    tt(h_lo[r0:r0 + VDIM, hm // 2, :], bank[hm // 2 % 2][r0:r0 + VDIM, :],
                       h_hi[r0:r0 + VDIM, hm // 2, :].bitcast(F32), SUB).then_inc(s_ml, 1)
            for m in range(KD):
                if m < KD - 1:
                    lo_after(U_OUT + m)
                residual(2, m, U_OUT + m + 1)
            root(2, 2)
            normalise(2)
            dve_lo(dve, lambda k: F2 + 3)
            ffn(F2, 1, 3)

        @block.gpsimd
        def _(pool):
            tt, ts = nc.gpsimd.tensor_tensor, nc.gpsimd.tensor_scalar

            def h_split(p):
                for m in range(KD):
                    pool.wait_ge(s_hh[p], m + 1)
                    tt(h_lo[:, m, :], act_t[:, m % 2, :], h_hi[:, m, :].bitcast(F32), SUB)\
                        .then_inc(s_hl[p], 1)
                for m in range(KD):
                    ts(x[:, m, :], x[:, m, :], ag[:, p, m:m + 1], ab[:, p, m:m + 1], MUL, ADD)\
                        .then_inc(s_res[p], 1)

            def a_split(f, a_hi, a_lo, i, lo, hi):
                for ff in range(2):
                    pool.wait_ge(s_ah[f], affine(lambda k: 2 * k + ff + 1, i, lo, hi))
                    t = affine(lambda k: 2 * k + ff, i, lo, hi)
                    if isinstance(i, int):
                        hi_, lo_ = a_hi[:, t, :], a_lo[:, t, :]
                    else:
                        hi_, lo_ = (z[:, bass.ds(t, 1), :].rearrange("p a n -> p (a n)")
                                    for z in (a_hi, a_lo))
                    tt(lo_, act_t[:, ff, :], hi_.bitcast(F32), SUB).then_inc(s_al[f], 1)

            def sums(p):
                pool.wait_ge(s_cc[p], 1)
                pool.wait_ge(s_res[p - 1], KD)
                for m in range(KD):
                    tt(x[:, m, :], x[:, m, :], shift[:], SUB).then_inc(s_xs[p], 1)
                for m in range(1, KD - 1):
                    pool.wait_ge(s_e[p], m + 1)
                    if m == 1:
                        pool.wait_ge(s_xs[p], 1)
                        tt(s_sum[:], x[:, 0, :], x[:, 1, :], ADD).then_inc(s_acc[p], 1)
                    else:
                        pool.wait_ge(s_acc[p], 2 * m - 2)
                        tt(s_sum[:], s_sum[:], x[:, m, :], ADD).then_inc(s_acc[p], 1)
                    pool.wait_ge(s_sq[p], m + 1)
                    tt(q_sum[:], q_sum[:], sq[:, m % 2, :], ADD).then_inc(s_acc[p], 1)

            def ffn(f, p, a_hi, a_lo):
                with pool.Fori(0, FT // 2) as i:
                    a_split(f, a_hi, a_lo, i, 0, FT // 2)
                sums(p)

            nc.gpsimd.memset(ones_t[:], 1.0 / P).then_inc(s_ones, 1)
            nc.gpsimd.memset(ones_d[:], 1.0 / D).then_inc(s_ones, 1)
            nc.gpsimd.memset(halfpi[:], math.pi / 2).then_inc(s_ones, 1)
            h_split(0)
            ffn(0, 1, a_hi1, a_lo1)
            h_split(1)

            pool.wait_ge(s_hl[1], KD)
            nc.gpsimd.memset(u[:, :, 0:PADW], 0.0).then_inc(s_pad, 1)
            pool.wait_ge(s_eva, 2)
            tt(s_sum[:], s_sum[:], sq[:, 0, :], ADD).then_inc(s_msum, 1)
            pool.wait_ge(s_eva, 4)
            tt(q_sum[:], q_sum[:], sq[:, 1, :], ADD).then_inc(s_msum, 1)
            for j in range(KKV):
                pool.wait_ge(s_lh, j + 1)
                tt(ckvn_lo[:, j, :], ckv[:, j, :], ckvn_hi[:, j, :].bitcast(F32), SUB)\
                    .then_inc(s_ll, 1)
            for j in (2, 3):
                pool.wait_ge(s_eva, 3 + j)
                pool.wait_ge(s_msum, j)
                tt(q_sum[:], q_sum[:], sq[:, j % 2, :], ADD).then_inc(s_msum, 1)

            nwin = [0]

            def win(ins):
                ins.then_inc(s_win, 1)
                nwin[0] += 1
                pool.wait_ge(s_win, nwin[0])

            def windows(g):
                pool.wait_ge(s_pad, 1)
                pool.wait_ge(s_evd, 2 + g)
                src, end = u[:, g, :], PADW + TOK
                for d in range(g + 1):
                    s, dst = 1 << d, wsum[:, d % 2, :]
                    win(tt(dst[:, 2 * s - 1:end], src[:, 2 * s - 1:end], src[:, s - 1:end - s], ADD))
                    src = dst
                wn, mean = WINDOWS[g], wsum[:, (g + 1) % 2, :]
                win(ts(mean[:, PADW:], src[:, PADW:], 1.0 / wn, 0.0, MUL, ADD))
                win(tt(mean[:, PADW:PADW + wn], src[:, PADW:PADW + wn],
                       cols[:, C_RCNT:C_RCNT + wn], MUL))
                win(tt(u[:, g, PADW:], mean[:, PADW:], u[:, g, PADW:], SUB))
                assert nwin[0] == POOLED[g]

            windows(0)
            for j in range(KQ):
                pool.wait_ge(s_lh, KKV + j + 1)
                tt(cqn_lo[:, j, :], cq[:, j, :], cqn_hi[:, j, :].bitcast(F32), SUB).then_inc(s_ll, 1)
            for g in range(1, NPG):
                windows(g)
            for hd in range(HEADS):
                pool.wait_ge(s_evd, sum("d" in b for b in BY[:T_Q + hd + 1]))
                tt(Q[64:96, hd, :], Q[64:96, hd, :], act_t[64:96, hd % 2, :], ADD).then_inc(s_q, 1)
            for g in range(NPG):
                pool.wait_ge(s_ph, g + 1)
                tt(h_lo[:, HEADS // 2 + g, :], act_t[:, g % 2, :],
                   h_hi[:, HEADS // 2 + g, :].bitcast(F32), SUB).then_inc(s_pl, 1)
            sums(2)
            h_split(2)
            ffn(1, 3, a_hi2, a_lo2)


def kernel(**inputs):
    import concourse.bacc as bacc
    from concourse.bass_utils import run_bass_kernel_spmd

    a = {k: np.asarray(v) for k, v in inputs.items()}

    def tiles(w):
        k, n = w.shape
        return w.reshape(k // P, P, n // P, P).transpose(2, 1, 0, 3).reshape(n // P, P, k)

    units = np.zeros((UNITS, P, UNIT), np.float32)
    for base, w_in, w_out in ((F1, "ffn1_w_in", "ffn1_w_out"), (F2, "ffn2_w_in", "ffn2_w_out")):
        t = tiles(a[w_in][0])
        units[base:base + UP:2], units[base + 1:base + UP:2] = t[:FT], t[FT:]
        t = tiles(a[w_out][0])
        for j in range(DPM):
            part = t[:, :, j * UNIT:(j + 1) * UNIT]
            units[base + UP + j:base + UP + DOWN:DPM, :, :part.shape[2]] = part
    w_in = a["w_in"][0]
    swap = np.r_[ROPE // 2:ROPE, 0:ROPE // 2]
    kr = w_in[:, QR + KVR:QR + KVR + ROPE]
    kr = np.concatenate([np.zeros((D, NOPE), np.float32), kr, kr[:, swap]], 1)
    proj = np.concatenate([w_in[:, QR:QR + KVR], kr, w_in[:, :QR], w_in[:, QR + KVR + ROPE:]], 1)
    units[MX:MX + N_PROJ] = tiles(proj)
    ukv = a["w_ukv"][0].reshape(KKV, P, HEADS, NOPE + VDIM)
    units[U_KNOPE] = ukv[..., :NOPE].transpose(1, 0, 2, 3).reshape(P, UNIT)
    units[U_V] = ukv[..., NOPE:].transpose(1, 0, 2, 3).reshape(P, UNIT)
    uq = a["w_uq"][0].reshape(KQ, P, HEADS, NOPE + ROPE)
    uq = np.concatenate([uq, uq[..., NOPE:][..., swap]], 3)
    uq = uq.transpose(2, 1, 0, 3).reshape(HEADS // 2, 2, P, KQ * P)
    units[U_UQ:U_OUT] = uq.transpose(0, 2, 1, 3).reshape(HEADS // 2, P, UNIT)
    units[U_OUT:F2] = tiles(a["w_out"][0])

    def by_tile(v):
        return v.reshape(-1, P).T

    rows = np.arange(P)
    freq = np.float32(10000.0) ** (-np.arange(0, ROPE, 2, dtype=np.float32) / np.float32(ROPE))
    const = np.concatenate([
        freq[rows % (ROPE // 2)][:, None],
        np.where(rows % ROPE < ROPE // 2, -1.0, 1.0)[:, None],
        np.tile(1.0 / np.arange(1, PADW + 1), (P, 1)), np.eye(P)], 1).astype(np.float32)
    cols = np.concatenate([
        by_tile(a["ln_in_g"]), by_tile(a["post_ln_g"][0]), by_tile(a["ln_in_b"]),
        by_tile(a["post_ln_b"][0]), by_tile(a["b_ada"][0]), by_tile(a["q_norm_g"][0]),
        by_tile(a["kv_norm_g"][0]), by_tile(a["pool_b"][0]), by_tile(a["pool_scale"][0]), const], 1)
    arrays = {
        "xT": a["x"][0].T.reshape(KD, P, TOK),
        "wunits": units,
        "ada_w": a["w_ada"][0].T.reshape(ADA, P, D),
        "c_rows": np.broadcast_to(a["c"][0], (P, D)),
        "pos_rows": np.broadcast_to(a["positions"][0], (P, TOK)),
        "cols_in": cols,
        "pool_w": a["pool_w"][0].transpose(1, 0, 2).reshape(P, NPG * P),
    }
    arrays = {k: np.ascontiguousarray(v) for k, v in arrays.items()}
    nc = bacc.Bacc("TRN2", target_bir_lowering=False, num_devices=1, dynamic_dma_scratch_size=2048)
    args = [nc.dram_tensor(k, v.shape, mybir.dt.from_np(v.dtype), kind="ExternalInput").ap()
            for k, v in arrays.items()]
    args.append(nc.dram_tensor("outT", (KD, P, TOK), mybir.dt.float32, kind="ExternalOutput").ap())
    build(nc, *args)
    out = run_bass_kernel_spmd(nc, [arrays], core_ids=[0]).results[0]["outT"]
    return np.ascontiguousarray(out.reshape(D, TOK).T).reshape(1, TOK, D)
```
